# Optimizing a Trainium2 kernel written in Bass

```python
import functools
import jax
import jax.numpy as jnp
from jax import lax
import numpy as np

D_MODEL = 1024
BATCH = 1
SEQ = 512
DEPTH = 2
DEC_BATCH = 8
DEC_SEQ = 4
PAST_LEN = 2048
PAGE_SIZE = 128

N_AB = (DEPTH + 1) // 2
N_C = DEPTH // 2

CONV_W = D_MODEL // 2
CONV_K = 3
N_HEADS = 8
NOPE_DIM = 64
ROPE_DIM = 32
V_DIM = 64
KV_RANK = 256
Q_RANK = 384
ROPE_THETA = 10000.0
ATTN_SCALE = (NOPE_DIM + ROPE_DIM) ** -0.5
Q_BLOCK = 128
MIX_WIDTH_AB = CONV_W + N_HEADS * V_DIM
IN_AB = 3 * CONV_W + Q_RANK + KV_RANK + ROPE_DIM
CHUNK = 128
GMLP_WIDTH = D_MODEL
GMLP_GROUPS = 8
GMLP_GROUP_W = GMLP_WIDTH // GMLP_GROUPS
D_FF = 4 * D_MODEL
PLE_DIM = 256
EPS = 1e-6

kernel_name = 'hybrid_conv_mla_gmlp_decoder_step'

def _rms(x, g):
    xf = x.astype(jnp.float32)
    y = xf * lax.rsqrt(jnp.mean(xf * xf, axis=-1, keepdims=True) + EPS)
    return (y * g.astype(jnp.float32)).astype(x.dtype)

def _split_last(z, sizes):
    parts, off = [], 0
    for s in sizes:
        parts.append(z[..., off:off + s])
        off += s
    return parts

def _rope_tables(pos):
    inv = ROPE_THETA ** (-jnp.arange(0, ROPE_DIM, 2, dtype=jnp.float32) / ROPE_DIM)
    ang = pos.astype(jnp.float32)[:, None] * inv[None, :]
    return jnp.cos(ang), jnp.sin(ang)

def _rope(x, cos, sin):
    half = ROPE_DIM // 2
    shape = (1, cos.shape[0]) + (1,) * (x.ndim - 3) + (half,)
    c = cos.reshape(shape)
    s = sin.reshape(shape)
    xf = x.astype(jnp.float32)
    x1, x2 = xf[..., :half], xf[..., half:]
    return jnp.concatenate([x1 * c - x2 * s, x2 * c + x1 * s], axis=-1).astype(x.dtype)

def _mla_attend_causal(q_lat, q_pe, ckv, kpe):
    b, t, h, r = q_lat.shape
    n_blk = t // Q_BLOCK
    qb = q_lat.reshape(b, n_blk, Q_BLOCK, h, r).transpose(1, 0, 2, 3, 4)
    pb = q_pe.reshape(b, n_blk, Q_BLOCK, h, ROPE_DIM).transpose(1, 0, 2, 3, 4)
    kpos = jnp.arange(t)

    def block(args):
        ql, qp, i = args
        s = jnp.einsum('bqhr,bkr->bhqk', ql, ckv) + jnp.einsum('bqhp,bkp->bhqk', qp, kpe)
        qpos = i * Q_BLOCK + jnp.arange(Q_BLOCK)
        s = jnp.where(kpos[None, :] <= qpos[:, None], s.astype(jnp.float32) * ATTN_SCALE, -jnp.inf)
        pr = jax.nn.softmax(s, axis=-1).astype(ckv.dtype)
        return jnp.einsum('bhqk,bkr->bqhr', pr, ckv)

    o = lax.map(block, (qb, pb, jnp.arange(n_blk)))
    return o.transpose(1, 0, 2, 3, 4).reshape(b, t, h, r)

def _mla_attend_paged(q_lat, q_pe, ckv, kpe, pool_ckv, pool_kpe, page_table):
    b, t, h, r = q_lat.shape
    past_c = pool_ckv[page_table]
    past_p = pool_kpe[page_table]
    n_pages, page = past_c.shape[1], past_c.shape[2]
    n_past = n_pages * page
    s_past = (jnp.einsum('bthr,bnsr->bhtns', q_lat, past_c)
              + jnp.einsum('bthp,bnsp->bhtns', q_pe, past_p)).reshape(b, h, t, n_past)
    s_new = jnp.einsum('bthr,bkr->bhtk', q_lat, ckv) + jnp.einsum('bthp,bkp->bhtk', q_pe, kpe)
    causal = jnp.tril(jnp.ones((t, t), dtype=bool))
    s_new = jnp.where(causal, s_new.astype(jnp.float32) * ATTN_SCALE, -jnp.inf)
    s = jnp.concatenate([s_past.astype(jnp.float32) * ATTN_SCALE, s_new], axis=-1)
    pr = jax.nn.softmax(s, axis=-1).astype(ckv.dtype)
    pr_past = pr[..., :n_past].reshape(b, h, t, n_pages, page)
    return (jnp.einsum('bhtns,bnsr->bthr', pr_past, past_c)
            + jnp.einsum('bhtk,bkr->bthr', pr[..., n_past:], ckv))

def _conv_mla_mixer(a, conv_prev, cos, sin, w_in, conv_w, q_norm, w_uq, kv_norm, w_uk, w_uv, w_out, attend):
    b, t, _ = a.shape
    hc, gc, gb, cq, ckv, kpe = _split_last(a @ w_in, (CONV_W, CONV_W, CONV_W, Q_RANK, KV_RANK, ROPE_DIM))
    up = jnp.concatenate([conv_prev, gc * hc], axis=1)
    conv = conv_w[0] * up[:, 0:t]
    for k in range(1, CONV_K):
        conv = conv + conv_w[k] * up[:, k:k + t]
    y_conv = gb * conv
    conv_state = up[:, t:]
    ckv = _rms(ckv, kv_norm)
    kpe = _rope(kpe, cos, sin)
    q = (_rms(cq, q_norm) @ w_uq).reshape(b, t, N_HEADS, NOPE_DIM + ROPE_DIM)
    q_nope = q[..., :NOPE_DIM]
    q_pe = _rope(q[..., NOPE_DIM:], cos, sin)
    q_lat = jnp.einsum('bthn,rhn->bthr', q_nope, w_uk)
    o_lat = attend(q_lat, q_pe, ckv, kpe)
    y_att = jnp.einsum('bthr,rhv->bthv', o_lat, w_uv).reshape(b, t, N_HEADS * V_DIM)
    y = jnp.concatenate([y_conv, y_att], axis=-1) @ w_out
    return y, conv_state, ckv, kpe

def _chunk_gmlp_mixer(a, w_in, v_norm, w_s, b_s, w_out):
    b, t, _ = a.shape
    z = jax.nn.gelu(a @ w_in, approximate=False)
    u = z[..., :GMLP_WIDTH]
    v = _rms(z[..., GMLP_WIDTH:], v_norm)
    n_chunks = -(-t // CHUNK)
    vp = jnp.pad(v, ((0, 0), (0, n_chunks * CHUNK - t), (0, 0)))
    vp = vp.reshape(b, n_chunks, CHUNK, GMLP_GROUPS, GMLP_GROUP_W)
    ws = jnp.where(jnp.tril(jnp.ones((CHUNK, CHUNK), dtype=bool)), w_s, jnp.zeros_like(w_s))
    s = jnp.einsum('gts,bcsgd->bctgd', ws, vp) + b_s.T[None, None, :, :, None]
    s = s.reshape(b, n_chunks * CHUNK, GMLP_WIDTH)[:, :t]
    return (u * s) @ w_out, v

def _sqrelu_mlp(a, w1, w2):
    hid = jnp.maximum(a @ w1, 0)
    return (hid * hid) @ w2

def _trunk(x, p, pos0, conv_prev, attend_fns, prm):
    b, t, _ = x.shape
    cos, sin = _rope_tables(pos0 + jnp.arange(t, dtype=jnp.int32))
    h = x
    conv_out, ckv_out, kpe_out, v_out = [], [], [], []
    for i in range(DEPTH):
        j = i // 2
        a = _rms(h, prm['norm_mix'][i])
        if i % 2 == 0:
            y, cs, ckv, kpe = _conv_mla_mixer(
                a, conv_prev[j], cos, sin, prm['w_in_ab'][j], prm['conv_w'][j], prm['q_norm'][j],
                prm['w_uq'][j], prm['kv_norm'][j], prm['w_uk'][j], prm['w_uv'][j], prm['w_out_ab'][j],
                attend_fns[j])
            conv_out.append(cs)
            ckv_out.append(ckv)
            kpe_out.append(kpe)
        else:
            y, v = _chunk_gmlp_mixer(a, prm['w_in_c'][j], prm['v_norm'][j], prm['w_s'][j],
                                     prm['b_s'][j], prm['w_out_c'][j])
            v_out.append(v)
        h = h + y
        h = h + _sqrelu_mlp(_rms(h, prm['norm_ffn'][i]), prm['w_ff1'][i], prm['w_ff2'][i])
        gate = jax.nn.sigmoid(_rms(h, prm['norm_ple'][i]) @ prm['w_ple_gate'][i])
        h = h + gate * (p[i] @ prm['w_ple'][i])
    return _rms(h, prm['norm_f']), conv_out, ckv_out, kpe_out, v_out

def setup_inputs(seed: int = 0) -> dict:
    key = jax.random.key(seed)
    k = jax.random.split(key, 29)
    f32 = jnp.float32

    def nrm(kk, shape, scale):
        return jax.random.normal(kk, shape, f32) * scale

    def gain(kk, shape):
        return 1.0 + 0.05 * jax.random.normal(kk, shape, f32)

    n_pages = PAST_LEN // PAGE_SIZE
    n_used = DEC_BATCH * n_pages
    n_pool = n_used + n_used // 4
    page_table = jax.random.permutation(k[5], n_pool)[:n_used].reshape(DEC_BATCH, n_pages).astype(jnp.int32)
    return {
        'x_prompt': nrm(k[0], (BATCH, SEQ, D_MODEL), 1.0),
        'x_sample': nrm(k[1], (DEC_BATCH, DEC_SEQ, D_MODEL), 1.0),
        'cache_ckv': nrm(k[2], (N_AB, n_pool, PAGE_SIZE, KV_RANK), 1.0),
        'cache_kpe': nrm(k[3], (N_AB, n_pool, PAGE_SIZE, ROPE_DIM), 1.0),
        'state_conv': nrm(k[4], (N_AB, DEC_BATCH, CONV_K - 1, CONV_W), 1.0),
        'page_table': page_table,
        'p_prompt': nrm(k[6], (DEPTH, BATCH, SEQ, PLE_DIM), 1.0),
        'p_sample': nrm(k[7], (DEPTH, DEC_BATCH, DEC_SEQ, PLE_DIM), 1.0),
        'norm_mix': gain(k[8], (DEPTH, D_MODEL)),
        'w_in_ab': nrm(k[9], (N_AB, D_MODEL, IN_AB), D_MODEL ** -0.5),
        'conv_w': nrm(k[10], (N_AB, CONV_K, CONV_W), CONV_K ** -0.5),
        'q_norm': gain(k[11], (N_AB, Q_RANK)),
        'w_uq': nrm(k[12], (N_AB, Q_RANK, N_HEADS * (NOPE_DIM + ROPE_DIM)), Q_RANK ** -0.5),
        'kv_norm': gain(k[13], (N_AB, KV_RANK)),
        'w_uk': nrm(k[14], (N_AB, KV_RANK, N_HEADS, NOPE_DIM), KV_RANK ** -0.5),
        'w_uv': nrm(k[15], (N_AB, KV_RANK, N_HEADS, V_DIM), KV_RANK ** -0.5),
        'w_out_ab': nrm(k[16], (N_AB, MIX_WIDTH_AB, D_MODEL), MIX_WIDTH_AB ** -0.5),
        'w_in_c': nrm(k[17], (N_C, D_MODEL, 2 * GMLP_WIDTH), D_MODEL ** -0.5),
        'v_norm': gain(k[18], (N_C, GMLP_WIDTH)),
        'w_s': nrm(k[19], (N_C, GMLP_GROUPS, CHUNK, CHUNK), CHUNK ** -0.5),
        'b_s': 1.0 + 0.02 * jax.random.normal(k[20], (N_C, GMLP_GROUPS, CHUNK), f32),
        'w_out_c': nrm(k[21], (N_C, GMLP_WIDTH, D_MODEL), GMLP_WIDTH ** -0.5),
        'norm_ffn': gain(k[22], (DEPTH, D_MODEL)),
        'w_ff1': nrm(k[23], (DEPTH, D_MODEL, D_FF), D_MODEL ** -0.5),
        'w_ff2': nrm(k[24], (DEPTH, D_FF, D_MODEL), D_FF ** -0.5),
        'norm_ple': gain(k[25], (DEPTH, D_MODEL)),
        'w_ple_gate': nrm(k[26], (DEPTH, D_MODEL, D_MODEL), D_MODEL ** -0.5),
        'w_ple': nrm(k[27], (DEPTH, PLE_DIM, D_MODEL), PLE_DIM ** -0.5),
        'norm_f': gain(k[28], (D_MODEL,)),
    }

def reference(x_prompt, x_sample, cache_ckv, cache_kpe, state_conv, page_table, p_prompt, p_sample,
              norm_mix, w_in_ab, conv_w, q_norm, w_uq, kv_norm, w_uk, w_uv, w_out_ab,
              w_in_c, v_norm, w_s, b_s, w_out_c, norm_ffn, w_ff1, w_ff2, norm_ple, w_ple_gate, w_ple, norm_f):
    prm = dict(norm_mix=norm_mix, w_in_ab=w_in_ab, conv_w=conv_w, q_norm=q_norm, w_uq=w_uq,
               kv_norm=kv_norm, w_uk=w_uk, w_uv=w_uv, w_out_ab=w_out_ab, w_in_c=w_in_c,
               v_norm=v_norm, w_s=w_s, b_s=b_s, w_out_c=w_out_c, norm_ffn=norm_ffn, w_ff1=w_ff1,
               w_ff2=w_ff2, norm_ple=norm_ple, w_ple_gate=w_ple_gate, w_ple=w_ple, norm_f=norm_f)
    conv_zero = jnp.zeros((x_prompt.shape[0], CONV_K - 1, CONV_W), x_prompt.dtype)
    y_prompt, conv_p, ckv_p, kpe_p, _ = _trunk(
        x_prompt, p_prompt, 0, [conv_zero] * N_AB, [_mla_attend_causal] * N_AB, prm)
    attend_s = [functools.partial(_mla_attend_paged, pool_ckv=cache_ckv[j], pool_kpe=cache_kpe[j],
                                  page_table=page_table) for j in range(N_AB)]
    y_sample, conv_s, ckv_s, kpe_s, v_s = _trunk(
        x_sample, p_sample, PAST_LEN, [state_conv[j] for j in range(N_AB)], attend_s, prm)
    conv_prompt = jnp.stack(conv_p)
    conv_sample = jnp.stack(conv_s)
    ckv_prompt = jnp.stack(ckv_p)
    kpe_prompt = jnp.stack(kpe_p)
    ckv_sample = jnp.stack(ckv_s)
    kpe_sample = jnp.stack(kpe_s)
    v_sample = jnp.stack(v_s)
    return (y_prompt, y_sample, conv_prompt, conv_sample, ckv_prompt, kpe_prompt, ckv_sample, kpe_sample, v_sample)


_drawn_inputs = setup_inputs


def setup_inputs(seed=0):
    import zlib

    import numpy as np

    out = dict(_drawn_inputs(seed))
    spreads = {}
    factors = {'cache_kpe': 4.731, 'q_norm': 8.0, 'b_s': 23.213, 'norm_ple': 20.516}
    for name, (base, spread) in spreads.items():
        noise = np.random.default_rng([zlib.crc32(name.encode()), seed]).standard_normal(out[name].shape)
        drawn = base * np.exp(spread * noise) if base else spread * noise
        out[name] = jnp.asarray(drawn.astype(out[name].dtype))
    for name, factor in factors.items():
        out[name] = (out[name] * factor).astype(out[name].dtype)
    return out
```

```python
from contextlib import ExitStack

import numpy as np
import concourse.bass as bass
from concourse import mybir

P = 128
D = 1024
KD = D // P
TP, NB, TD = 512, 8, 4
TS = NB * TD
T = TP + TS
TH = T // 2
CW, H, NOPE, ROPE, VD, R, QR = 512, 8, 64, 32, 64, 256, 384
PAGE, NPG, POOL, PAST = 128, 16, 160, 2048
DFF, PLE = 4096, 256
EPS = 1e-6
SCALE = float(NOPE + ROPE) ** -0.5
UNIT = 2048
SLOTS = 4
U_INAB, N_INAB = 0, 9
U_OUTAB = U_INAB + N_INAB
U_FFN = [U_OUTAB + 4, 0]
U_PLE = [U_FFN[0] + 32, 0]
U_INC = U_PLE[0] + 5
U_OUTC = U_INC + 8
U_FFN[1] = U_OUTC + 4
U_PLE[1] = U_FFN[1] + 32
N_UNITS = U_PLE[1] + 5
T_N0 = 0
T_INAB = 1
T_NQ = T_INAB + 18
T_NKV = T_NQ + 1
T_UQ = T_NKV + 1
T_UK = T_UQ + 8
T_UV = T_UK + 4
T_OUTAB = T_UV + 4
T_N1 = T_OUTAB + 8
T_FFN = [T_N1 + 1, 0]
T_PP = [T_FFN[0] + 64, 0]
T_NP = [T_PP[0] + 8, 0]
T_GATE = [T_NP[0] + 1, 0]
T_N3 = T_GATE[0] + 8
T_INC = T_N3 + 1
T_NV = T_INC + 16
T_SP = T_NV + 1
T_OUTC = T_SP + 16
T_N4 = T_OUTC + 8
T_FFN[1] = T_N4 + 1
T_PP[1] = T_FFN[1] + 64
T_NP[1] = T_PP[1] + 8
T_GATE[1] = T_NP[1] + 1
T_NF = T_GATE[1] + 8
H_OUTAB = 0
H_FFN = [8, 0]
H_GATE = [40, 0]
H_OUTC = 48
H_FFN[1] = 56
H_GATE[1] = 88
NPR = H * 4


def tiles_through(u):
    for first, tile, per in ((U_PLE[1] + 1, T_GATE[1], 2), (U_PLE[1], T_PP[1], 8), (U_FFN[1], T_FFN[1], 2),
                             (U_OUTC, T_OUTC, 2), (U_INC, T_INC, 2), (U_PLE[0] + 1, T_GATE[0], 2),
                             (U_PLE[0], T_PP[0], 8), (U_FFN[0], T_FFN[0], 2), (U_OUTAB, T_OUTAB, 2),
                             (U_INAB, T_INAB, 2)):
        if u >= first:
            return tile + per * (u - first + 1)


def build(nc, a):
    F = mybir.dt.float32
    ACT = mybir.ActivationFunctionType
    ALU = mybir.AluOpType
    AX = mybir.AxisListType.X
    ctx = ExitStack()
    with ctx:
        def sb(name, shape, dt=F):
            return ctx.enter_context(nc.sbuf_tensor(name, shape, dt))

        def sem(name):
            return ctx.enter_context(nc.semaphore(name))

        h = sb("h", [P, KD, T])
        A = sb("A", [P, KD, T])
        B = sb("B", [P, KD, T])
        XIN, HID = (A, B), (B, A)
        ring = sb("ring", [P, SLOTS, UNIT])
        rbuf = sb("rbuf", [P, 2, T])
        sq = sb("sq", [P, 2, T])
        ssum = sb("ssum", [P, T])
        rstd = sb("rstd", [P, T])
        stage = sb("stage", [P, 18, T])
        attw = sb("attw", [P, 6400])
        S = sb("S", [P, 10240])
        gains = sb("gains", [P, 84])
        ones = sb("ones", [P, P])
        ident = sb("ident", [P, P])
        masks = sb("masks", [P, 2 * P + 96])
        small = sb("small", [P, 48])
        pt = sb("pt_ids", [1, NB * NPG], mybir.dt.int32)
        psum = ctx.enter_context(nc.psum_tensor("psum", [P, 8, 512], F))

        gain = lambda n, k: gains[:, 8 * n + k:8 * n + k + 1]
        qgain = lambda k: gains[:, 64 + k:65 + k]
        kvgain = lambda k: gains[:, 67 + k:68 + k]
        tap = lambda i, c: gains[:, 69 + 4 * i + c:70 + 4 * i + c]
        cmask = masks[:, 0:P]
        smask = masks[:, P:P + 64].rearrange("p (g k) -> p g k", g=2)
        bmask = masks[0:32, P + 64:P + 96]
        tri = masks[:, P + 96:]
        wuq = attw[:, 0:3072].rearrange("p (k m) -> p k m", k=3)
        wuk = attw[:, 3072:4096].rearrange("p (k m) -> p k m", k=2)
        wuv = attw[:, 4096:5120].rearrange("p (k m) -> p k m", k=2)
        wukT = attw[0:64, 0:2048].rearrange("p (h r) -> p h r", h=H)
        wsS = attw[0:32, 0:256].rearrange("p (g t) -> p g t", g=8)
        wsT = attw[:, 256:1280].rearrange("p (g t) -> p g t", g=8)
        bias = attw[:, 1280:2560].rearrange("p (g t) -> p g t", g=8)
        wsM = attw[:, 2560:3584].rearrange("p (g t) -> p g t", g=8)
        wsSM = attw[0:32, 3584:3840].rearrange("p (g t) -> p g t", g=8)
        up = S[:, 0:2248].rearrange("p (c t) -> p c t", c=4)
        UPS = TP + 2
        acc = S[:, 2304:2304 + T]
        ups = lambda c, o, n: up[:, c, UPS:UPS + 48].rearrange("p (b t) -> p b t", b=NB)[:, :, o:o + n]
        tok = lambda x: x.rearrange("p (b t) -> p b t", b=NB)
        kT = S[:, 0:4096].rearrange("p (c n) -> p c n", c=2)
        kpT = S[64:96, 4096:6144]
        V = S[:, 6144:10240].rearrange("p (g r) -> p g r", g=NPG)
        rope = B
        Q = A
        flat = stage[:, :, :].rearrange("p c t -> p (c t)")
        K = flat[:, 0:4096].rearrange("p (h n) -> p h n", h=H)
        vtok = flat[:, 4096:6144].rearrange("p (i n) -> p i n", i=4)
        ckv_tok = flat[0:32, 6144:6400]
        PW = PAST + 32
        Ps = flat[:, 0:PW]
        PTs = flat[:, PW:PW + 2176].rearrange("p (g r) -> p g r", g=17)
        olat = flat[:, 4256:4256 + 512].rearrange("p (c r) -> p c r", c=2)
        qlat = sq[:, 0, 0:512].rearrange("p (c r) -> p c r", c=2)
        qpe = sq[64:96, 1, 0:256]
        kpe_new = sq[64:96, 1, 256:288]
        Pp = rbuf
        PTp = attw[:, 5376:6400].rearrange("p (i n) -> p i n", i=2)
        pp = stage
        v = S[:, 0:KD * T].rearrange("p (k t) -> p k t", k=KD)
        vtk = S[:, 4352:4352 + 4096].rearrange("p (i n) -> p i n", i=4)
        vts = S[0:32, 8448:8448 + 1024]
        pemb = S[:, 8448 + 512:8448 + 512 + 2 * T].rearrange("p (k t) -> p k t", k=2)

        slot = lambda t: psum[:, 2 * (t % 4):2 * (t % 4) + 2, :]
        halves = lambda x: x.rearrange("p (a t) -> p a t", a=2)
        pv = lambda t: slot(t)[:, :, 0:TH]

        w_loaded = [sem(f"w_loaded{i}") for i in range(SLOTS)]
        x_loaded = sem("x_loaded")
        c_loaded = sem("c_loaded")
        attw_loaded = sem("attw_loaded")
        ukT_loaded = sem("ukT_loaded")
        spw_loaded = sem("spw_loaded")
        pemb_loaded = sem("pemb_loaded")
        ids_loaded = sem("ids_loaded")
        kT_loaded = sem("kT_loaded")
        V_loaded = sem("V_loaded")
        consts = sem("consts")
        psum_full = sem("psum_full")
        psum_free = sem("psum_free")
        x_ready = sem("x_ready")
        sq_ready = sem("sq_ready")
        sum_step = sem("sum_step")
        var_ready = sem("var_ready")
        root_done = sem("root_done")
        rstd_done = sem("rstd_done")
        h_done = sem("h_done")
        hid_ready = sem("hid_ready")
        act_x = sem("act_x")
        dve_x = sem("dve_x")
        conv_done = sem("conv_done")
        sc_full = sem("sc_full")
        pmax = sem("pmax")
        pexp = sem("pexp")
        pnorm = sem("pnorm")
        pt_full = sem("pt_full")
        pt_ready = sem("pt_ready")
        y_full = sem("y_full")
        y_free = sem("y_free")
        ql_full = sem("ql_full")
        ql_ready = sem("ql_ready")
        kT_used = sem("kT_used")
        s_full = sem("s_full")
        s_soft = sem("s_soft")
        st_full = sem("st_full")
        st_ready = sem("st_ready")
        so_full = sem("so_full")
        so_ready = sem("so_ready")
        sy_full = sem("sy_full")
        sy_ready = sem("sy_ready")
        stored = sem("stored")
        block = ctx.enter_context(nc.Block())

        @block.sync
        def _(sp):
            sp.dma_start(h[:], a["xT"].rearrange("(k p) t -> p k t", p=P)).then_inc(x_loaded, 16)
            sp.dma_start(gains[:], a["gains"]).then_inc(c_loaded, 16)
            sp.dma_start(ident[:], a["ident"]).then_inc(c_loaded, 16)
            sp.dma_start(masks[:], a["masks"]).then_inc(c_loaded, 16)
            sp.dma_start(rope[:, 4:6, :], a["rope"]).then_inc(c_loaded, 16)
            for c in range(4):
                sp.dma_start(ups(c, 0, 2), a["state"][:, c]).then_inc(c_loaded, 16)

            def unit(u):
                if u >= SLOTS:
                    sp.wait_ge(psum_full, tiles_through(u - SLOTS))
                sp.dma_start(ring[:, u % SLOTS, :], a["weights"][u]).then_inc(w_loaded[u % SLOTS], 16)

            for u in range(4):
                unit(u)
            sp.dma_start(attw[:, 0:5120], a["attw"]).then_inc(attw_loaded, 16)
            sp.dma_start(pt[:], a["page_table"]).then_inc(ids_loaded, 16)
            for u in range(4, U_OUTAB + 4):
                unit(u)
            sp.wait_ge(dve_x, 4)
            sp.dma_start(a["ckvT"].rearrange("(k p) t -> p k t", p=P), stage[:, 15:17, :]).then_inc(stored, 16)
            sp.wait_ge(conv_done, 1)
            sp.dma_start(a["kpeT"], ssum[64:96, :]).then_inc(stored, 16)
            sp.dma_start(a["convp"], up[:, :, TP:TP + 2]).then_inc(stored, 16)
            for c in range(4):
                sp.dma_start(a["convs"][:, c], ups(c, 4, 2)).then_inc(stored, 16)
            sp.wait_ge(psum_full, T_UK)
            sp.dma_start(wukT, a["wukT"]).then_inc(ukT_loaded, 16)
            sp.wait_ge(stored, 112)
            sp.wait_ge(ids_loaded, 16)
            for b in range(NB):
                if b:
                    sp.wait_ge(kT_used, b)
                with nc.Fori(0, NPG, engines=[sp.engine]) as g:
                    page = sp.value_load(pt[0:1, bass.ds(g + NPG * b, 1)], min_val=0, max_val=POOL - 1)
                    sp.dma_start(kT[:, :, bass.ds(g * PAGE, PAGE)],
                                 a["keysT"][bass.ds(page, 1), :, :].rearrange("o p (c n) -> p (o c) n", c=2))\
                      .then_inc(kT_loaded, 16)
                    sp.dma_start(kpT[:, bass.ds(g * PAGE, PAGE)],
                                 a["kpesT"][bass.ds(page, 1), :, :].rearrange("o p n -> p (o n)")).then_inc(kT_loaded, 16)
                if b == 3 or b == 7:
                    for bb in range(b - 3, b + 1):
                        if bb:
                            sp.wait_ge(so_full, bb)
                        with nc.Fori(0, NPG, engines=[sp.engine]) as g:
                            page = sp.value_load(pt[0:1, bass.ds(g + NPG * bb, 1)], min_val=0, max_val=POOL - 1)
                            sp.dma_start(V[:, bass.ds(g, 1), :],
                                         a["rows"][bass.ds(page, 1), :, :].rearrange("o p r -> p o r"))\
                              .then_inc(V_loaded, 16)
            def ffn_units(u0):
                for u in range(u0, u0 + 4):
                    unit(u)
                with nc.Fori(1, 8, engines=[sp.engine]) as i:
                    for j in range(4):
                        u = u0 + j
                        sp.wait_ge(psum_full, i * 8 + (tiles_through(u) - 8))
                        sp.dma_start(ring[:, u % SLOTS, :],
                                     a["weights"][bass.ds(i * 4 + u, 1), :, :].rearrange("o p n -> p (o n)"))\
                          .then_inc(w_loaded[u % SLOTS], 16)

            ffn_units(U_FFN[0])
            sp.dma_start(pemb[:], a["pemb"][0]).then_inc(pemb_loaded, 16)
            for u in range(U_PLE[0], U_FFN[1]):
                unit(u)
                if u == U_INC:
                    sp.wait_ge(psum_full, T_NP[0])
                    sp.dma_start(wsS, a["wsS"]).then_inc(spw_loaded, 16)
                    sp.dma_start(wsT, a["wsT"]).then_inc(spw_loaded, 16)
                    sp.dma_start(attw[:, 1280:2560], a["bias"].to_broadcast([P, 1280])).then_inc(spw_loaded, 16)
            sp.wait_ge(dve_x, 5)
            sp.dma_start(a["vT"].rearrange("(k p) t -> p k t", p=P), v[:, :, TP:T]).then_inc(stored, 16)
            ffn_units(U_FFN[1])
            sp.wait_ge(psum_full, T_OUTC)
            sp.wait_ge(stored, 128)
            sp.dma_start(pemb[:], a["pemb"][1]).then_inc(pemb_loaded, 16)
            for u in range(U_PLE[1], N_UNITS):
                unit(u)
            for m in range(KD):
                sp.wait_ge(dve_x, 6 + m)
                sp.dma_start(a["yT"][m * P:(m + 1) * P, :], A[:, m, :]).then_inc(stored, 16)
            sp.wait_ge(stored, 128 + 16 * KD)

        @block.gpsimd
        def _(pool):
            pool.memset(ones[:], 1.0).then_inc(consts, 1)
            pool.memset(up[:, :, 0:2], 0.0).then_inc(consts, 1)

        @block.tensor
        def _(pe):
            def free(t):
                if t >= 4:
                    pe.wait_ge(psum_free, t - 3)

            def ones_tile(t, chunks):
                free(t)
                for n, c in enumerate(chunks):
                    for i in range(2):
                        last = pe.matmul(slot(t)[:, i, 0:TH], ones[:], c[:, TH * i:TH * i + TH],
                                         start=n == 0, stop=n == len(chunks) - 1)
                last.then_inc(psum_full, 1)

            def tile(t, lhs, x, ks, x_sem=None, x_base=0, q=None, q_tiles=0, q_x=0):
                if q is None:
                    free(t)
                else:
                    pe.wait_ge(psum_free, q * q_tiles + (t - 3))
                for k in range(ks):
                    if x_sem is not None:
                        pe.wait_ge(x_sem, x_base + k + 1 if q is None or not q_x else q * q_x + (x_base + k + 1))
                    for i in range(2):
                        w = lhs(k)
                        last = pe.matmul(slot(t)[0:w.shape[-1], i, 0:TH], w, x[:, k, TH * i:TH * i + TH],
                                         start=k == 0, stop=k == ks - 1)
                last.then_inc(psum_full, 1)
                return last

            def unit_tiles(u, t, n, x, x_sem, x_base, q=None, q_x=0):
                if q is None:
                    pe.wait_ge(w_loaded[u % SLOTS], 16 * (u // SLOTS + 1))
                else:
                    pe.wait_ge(w_loaded[u % SLOTS], q * 32 + 16 * (u // SLOTS + 1))
                w = ring[:, u % SLOTS, :].rearrange("p (k m) -> p k m", k=KD)
                for j in range(n):
                    tile(t + j, lambda k: w[:, k, j * P:(j + 1) * P], x, KD, x_sem, x_base, q, 16, q_x)

            def ffn(l):
                with nc.Fori(0, 4, engines=[pe.engine]) as q:
                    for j in range(4):
                        unit_tiles(U_FFN[l] + j, T_FFN[l] + 2 * j, 2, XIN[l], x_ready, 8 * (1 + 3 * l), q)
                    for j in range(4):
                        unit_tiles(U_FFN[l] + 4 + j, T_FFN[l] + 8 + 2 * j, 2, HID[l], hid_ready, 32 * l, q, 8)

            def ple(l):
                u = U_PLE[l]
                pe.wait_ge(pemb_loaded, 16 * (l + 1))
                pe.wait_ge(w_loaded[u % SLOTS], 16 * (u // SLOTS + 1))
                w = ring[:, u % SLOTS, :].rearrange("p (k m) -> p k m", k=2)
                for m in range(8):
                    tile(T_PP[l] + m, lambda k: w[:, k, m * P:(m + 1) * P], pemb, 2)
                pe.wait_ge(sum_step, 8 * (3 + 3 * l))
                ones_tile(T_NP[l], [ssum[:, :]])
                for j in range(4):
                    unit_tiles(u + 1 + j, T_GATE[l] + 2 * j, 2, XIN[l], x_ready, 8 * (2 + 3 * l))

            pe.wait_ge(consts, 2)
            pe.wait_ge(sum_step, 8)
            ones_tile(T_N0, [ssum[:, :]])
            for j in range(N_INAB):
                unit_tiles(U_INAB + j, T_INAB + 2 * j, 2, A, x_ready, 0)
            pe.wait_ge(act_x, 5)
            ones_tile(T_NQ, [A[:, i, :] for i in range(3)])
            ones_tile(T_NKV, [A[:, i, :] for i in range(3, 5)])
            pe.wait_ge(attw_loaded, 16)
            pe.wait_ge(dve_x, 4)
            for m in range(8):
                tile(T_UQ + m, lambda k: wuq[:, k, m * P:(m + 1) * P], stage[:, 12:15, :], 3)
            for m in range(4):
                t = T_UK + m
                free(t)
                for k in range(2):
                    last = pe.matmul(slot(t)[:, 0, :], wuk[:, k, m * P:(m + 1) * P], stage[:, 15 + k, 0:TP],
                                     start=k == 0, stop=k == 1)
                last.then_inc(psum_full, 1)
            for i in range(4):
                t = T_UV + i
                free(t)
                for k in range(2):
                    last = pe.matmul(slot(t)[:, 0, :], stage[:, 15 + k, i * P:(i + 1) * P], wuv[:, k, :],
                                     start=k == 0, stop=k == 1)
                last.then_inc(psum_full, 1)

            pe.wait_ge(psum_free, T_OUTAB)
            pe.wait_ge(conv_done, 1)
            for n in range(NPR + 2):
                if n < NPR:
                    hd, i = divmod(n, 4)
                    if n >= 3:
                        pe.wait_ge(pexp, n - 2)
                    pe.matmul(psum[:, n % 3, 0:(i + 1) * P], Q[0:96, hd, i * P:(i + 1) * P],
                              K[0:96, hd, 0:(i + 1) * P], start=True, stop=True).then_inc(sc_full, 1)
                if n >= 2:
                    m = n - 2
                    hd, i = divmod(m, 4)
                    pe.wait_ge(pnorm, m + 1)
                    if m >= 2:
                        pe.wait_ge(pt_ready, m - 1)
                    for j in range(i + 1):
                        last = pe.transpose(psum[:, 3 + m % 2, j * P:(j + 1) * P],
                                            Pp[:, m % 2, j * P:(j + 1) * P], ident[:])
                    last.then_inc(pt_full, 1)
                    pe.wait_ge(pt_ready, m + 1)
                    if m >= 2:
                        pe.wait_ge(y_free, m - 1)
                    yb = psum[64 * (hd % 2):64 * (hd % 2) + 64, 5 + m % 2, 0:P]
                    for j in range(i + 1):
                        last = pe.matmul(yb, vtok[:, j, hd * VD:(hd + 1) * VD],
                                         PTp[:, m % 2, j * P:(j + 1) * P], start=j == 0, stop=j == i)
                    last.then_inc(y_full, 1)

            pe.wait_ge(y_free, NPR)
            pe.wait_ge(ukT_loaded, 16)
            for hd in range(H):
                for c in range(2):
                    last = pe.matmul(psum[:, c, hd * 32:(hd + 1) * 32], wukT[:, hd, c * P:(c + 1) * P],
                                     Q[0:64, hd, TP:T], start=True, stop=True)
            for c in range(2):
                last = pe.transpose(psum[0:32, 7, c * P:(c + 1) * P], stage[:, 15 + c, TP:T], ident[:])
            last.then_inc(ql_full, 1)
            pe.wait_ge(ql_ready, 3)
            for g in range(2):
                if g:
                    pe.wait_ge(s_soft, 4 * g)
                for bb in range(4):
                    b = 4 * g + bb
                    pe.wait_ge(kT_loaded, 32 * NPG * (b + 1))
                    rows = slice(32 * bb, 32 * bb + 32)
                    for kb in range(4):
                        keys = slice(kb * 512, kb * 512 + 512)
                        for c in range(2):
                            pe.matmul(psum[rows, kb, :], qlat[:, c, 32 * b:32 * b + 32], kT[:, c, keys],
                                      start=c == 0, stop=False)
                        last = pe.matmul(psum[rows, kb, :], qpe[:, 32 * b:32 * b + 32], kpT[:, keys],
                                         start=False, stop=True)
                    last.then_inc(kT_used, 1)
                for c in range(2):
                    pe.matmul(psum[:, 4, 0:32], qlat[:, c, P * g:P * g + P], stage[:, 15 + c, TP:T],
                              start=c == 0, stop=False)
                pe.matmul(psum[:, 4, 0:32], qpe[:, P * g:P * g + P], kpe_new, start=False, stop=True)\
                  .then_inc(s_full, 1)
                pe.wait_ge(s_soft, 4 * g + 4)
                for n in range(5):
                    m = 5 * g + n
                    if m >= 2:
                        pe.wait_ge(st_ready, m - 1)
                    for j in range(4 if n < 4 else 1):
                        pg = 4 * n + j
                        if pg < 16:
                            last = pe.transpose(psum[:, 5 + m % 2, j * P:(j + 1) * P],
                                                Ps[:, pg * P:(pg + 1) * P], ident[:])
                        else:
                            last = pe.transpose(psum[0:32, 5 + m % 2, 0:P], Ps[:, PAST:PAST + 32], ident[:])
                    last.then_inc(st_full, 1)
                pe.wait_ge(st_ready, 5 * g + 5)
                for bb in range(4):
                    b = 4 * g + bb
                    pe.wait_ge(V_loaded, 16 * NPG * (b + 1))
                    if b:
                        pe.wait_ge(so_ready, b)
                    cols = slice(32 * bb, 32 * bb + 32)
                    for c in range(2):
                        for pg in range(NPG):
                            pe.matmul(psum[:, 7, 32 * c:32 * c + 32], V[:, pg, c * P:(c + 1) * P], PTs[:, pg, cols],
                                      start=pg == 0, stop=False)
                        last = pe.matmul(psum[:, 7, 32 * c:32 * c + 32], ckv_tok[:, c * P:(c + 1) * P],
                                         PTs[0:32, 16, cols], start=False, stop=True)
                    last.then_inc(so_full, 1)
            pe.wait_ge(so_ready, 8)
            ol = olat.rearrange("p c (b h t) -> p c b h t", b=NB, h=H)
            for hd in range(H):
                for c in range(2):
                    last = pe.matmul(psum[64 * (hd % 2):64 * (hd % 2) + 64, 7, 32 * (hd // 2):32 * (hd // 2) + 32],
                                     wuv[:, c, hd * VD:(hd + 1) * VD], ol[:, c, :, hd, :],
                                     start=c == 0, stop=c == 1)
            last.then_inc(sy_full, 1)
            pe.wait_ge(sy_ready, 1)

            for j in range(4):
                unit_tiles(U_OUTAB + j, T_OUTAB + 2 * j, 2, B, None, 0)
            pe.wait_ge(sum_step, 16)
            ones_tile(T_N1, [ssum[:, :]])
            ffn(0)
            ple(0)
            pe.wait_ge(sum_step, 32)
            ones_tile(T_N3, [ssum[:, :]])
            for j in range(8):
                unit_tiles(U_INC + j, T_INC + 2 * j, 2, XIN[1], x_ready, 24)
            pe.wait_ge(act_x, 5 + 8 + 16 + 8)
            ones_tile(T_NV, [A[:, i, :] for i in range(8)])
            pe.wait_ge(dve_x, 5)
            for g in range(8):
                t = T_SP + 2 * g
                free(t)
                for i in range(4):
                    pe.transpose(slot(t)[:, 0, i * P:(i + 1) * P], v[:, g, i * P:(i + 1) * P], ident[:])
                pe.transpose(slot(t)[0:32, 1, 0:P], v[:, g, TP:T], ident[:]).then_inc(psum_full, 1)
                t += 1
                pe.wait_ge(psum_free, t)
                for i in range(4):
                    pe.matmul(slot(t)[:, 0, i * P:(i + 1) * P], vtk[:, i, g * P:(g + 1) * P], wsM[:, g, :],
                              start=True, stop=True)
                pe.matmul(slot(t)[:, 1, 0:32], vts[:, g * P:(g + 1) * P], wsSM[:, g, :],
                          start=True, stop=True).then_inc(psum_full, 1)
            pe.wait_ge(psum_free, T_OUTC)
            for j in range(4):
                unit_tiles(U_OUTC + j, T_OUTC + 2 * j, 2, HID[1], None, 0)
            pe.wait_ge(sum_step, 40)
            ones_tile(T_N4, [ssum[:, :]])
            ffn(1)
            ple(1)
            pe.wait_ge(sum_step, 56)
            ones_tile(T_NF, [ssum[:, :]])

        @block.scalar
        def _(act):
            def norm_chunk(n, h_base, X, m):
                if h_base is not None:
                    act.wait_ge(h_done, h_base + m + 1)
                act.activation(X[:, m, :], h[:, m, :], ACT.Copy, scale=gain(n, m)).then_inc(x_ready, 1)
                if 8 * n + m >= 2:
                    act.wait_ge(sum_step, 8 * n + m - 1)
                act.activation(sq[:, m % 2, :], h[:, m, :], ACT.Square).then_inc(sq_ready, 1)

            def norm_in(n, h_base, last_reader, X):
                if last_reader:
                    act.wait_ge(psum_full, last_reader)
                for m in range(KD):
                    norm_chunk(n, h_base, X, m)

            def root(n, x):
                act.wait_ge(var_ready, n + 1)
                act.activation(x, x, ACT.Sqrt).then_inc(root_done, 1)

            def hidden(l):
                with nc.Fori(0, 4, engines=[act.engine]) as q:
                    act.wait_ge(psum_full, q * 16 + T_FFN[l])
                    for j in range(8):
                        act.wait_ge(psum_free, q * 16 + (T_FFN[l] + j + 1))
                        act.activation(HID[l][:, j, :], rbuf[:, j % 2, :], ACT.Square).then_inc(hid_ready, 1)

            def gates(l):
                for m in range(9):
                    if m < 8:
                        act.wait_ge(psum_free, T_GATE[l] + m + 1)
                        act.activation(rbuf[:, m % 2, :], rbuf[:, m % 2, :], ACT.Sigmoid).then_inc(act_x, 1)
                    if m:
                        norm_chunk(3 + 3 * l, H_GATE[l], HID[l], m - 1)

            act.wait_ge(x_loaded, 16)
            act.wait_ge(c_loaded, 128)
            norm_in(0, None, 0, XIN[0])
            root(0, rstd[:])
            act.wait_ge(psum_full, T_NQ)
            act.wait_ge(psum_free, T_NQ)
            for i in range(5):
                act.activation(A[:, i, :], stage[:, 12 + i, :], ACT.Square).then_inc(act_x, 1)
            root(1, sq[:, 0, :])
            root(2, sq[:, 1, :])
            for n in range(NPR + 1):
                if n < NPR:
                    i = n % 4
                    act.wait_ge(pmax, n + 1)
                    if n >= 2:
                        act.wait_ge(pt_full, n - 1)
                    act.activation(Pp[:, n % 2, 0:(i + 1) * P], psum[:, n % 3, 0:(i + 1) * P], ACT.Exp,
                                   bias=small[:, 8 + n % 2:9 + n % 2], scale=SCALE,
                                   accum_out=small[:, 12 + n % 2:13 + n % 2]).then_inc(pexp, 1)
                if n >= 1:
                    m = n - 1
                    i = m % 4
                    act.wait_ge(pt_full, m + 1)
                    if m >= 2:
                        act.wait_ge(y_full, m - 1)
                    act.activation(PTp[:, m % 2, 0:(i + 1) * P], psum[:, 3 + m % 2, 0:(i + 1) * P], ACT.Copy)\
                       .then_inc(pt_ready, 1)
            for g in range(2):
                act.wait_ge(s_soft, 4 * g + 2)
                act.activation(Ps[:, 0:PAST].rearrange("p (a n) -> p a n", a=4), psum[:, 0:4, :], ACT.Exp,
                               bias=small[:, 20:21], scale=SCALE, accum_out=small[:, 22:23]).then_inc(pexp, 1)
                act.activation(Ps[:, PAST:PW], Ps[:, PAST:PW], ACT.Exp,
                               bias=small[:, 20:21], accum_out=small[:, 23:24]).then_inc(pexp, 1)
                for n in range(5):
                    m = 5 * g + n
                    act.wait_ge(st_full, m + 1)
                    if g:
                        act.wait_ge(so_full, 4 * g)
                    if n < 4:
                        act.activation(PTs[:, 4 * n:4 * n + 4, :],
                                       psum[:, 5 + m % 2, :].rearrange("p (a n) -> p a n", a=4), ACT.Copy)\
                           .then_inc(st_ready, 1)
                    else:
                        act.activation(PTs[0:32, 16, :], psum[0:32, 5 + m % 2, 0:P], ACT.Copy).then_inc(st_ready, 1)
            norm_in(1, H_OUTAB, T_NKV + 1, XIN[0])
            root(3, rstd[:])
            hidden(0)
            norm_in(2, H_FFN[0] + 24, T_FFN[0] + 56, XIN[0])
            root(4, rstd[:])
            gates(0)
            root(5, rstd[:])
            for m in range(16):
                act.wait_ge(psum_free, T_INC + m + 1)
                dst = stage[:, 8 + m, :] if m < 8 else v[:, m - 8, :]
                act.activation(dst, rbuf[:, m % 2, :], ACT.Gelu).then_inc(act_x, 1)
            act.wait_ge(psum_full, T_NV)
            act.wait_ge(act_x, 5 + 8 + 16)
            for m in range(8):
                act.activation(A[:, m, :], v[:, m, :], ACT.Square).then_inc(act_x, 1)
            root(6, sq[:, 0, :])
            norm_in(4, H_OUTC, T_NV + 1, XIN[1])
            root(7, rstd[:])
            hidden(1)
            norm_in(5, H_FFN[1] + 24, T_FFN[1] + 56, XIN[1])
            root(8, rstd[:])
            gates(1)
            root(9, rstd[:])

        @block.vector
        def _(dve):
            full = lambda t: dve.wait_ge(psum_full, t + 1)
            chain = sem("dve_chain")
            links = [0]

            def link(ins):
                links[0] += 1
                ins.then_inc(chain, 1)
                dve.wait_ge(chain, links[0])

            def sum_sq(n, m):
                dve.wait_ge(sq_ready, 8 * n + m + 1)
                if m:
                    dve.wait_ge(sum_step, 8 * n + m)
                    dve.tensor_tensor(ssum[:], ssum[:], sq[:, m % 2, :], ALU.add).then_inc(sum_step, 1)
                else:
                    dve.tensor_copy(ssum[:], sq[:, 0, :]).then_inc(sum_step, 1)

            def norm_root(n, t, x, width):
                full(t)
                dve.tensor_scalar(halves(x), pv(t), 1.0 / width, EPS, ALU.mult, ALU.add).then_inc(var_ready, 1)
                dve.wait_ge(var_ready, n + 1)
                dve.nop().then_inc(psum_free, 1)
                dve.wait_ge(root_done, n + 1)
                dve.reciprocal(x, x).then_inc(rstd_done, 1)
                dve.wait_ge(rstd_done, n + 1)

            def add_h(t0, base, n):
                for m in range(8):
                    full(t0 + m)
                    if base + m >= 8:
                        dve.wait_ge(h_done, base + m - 7)
                    dve.tensor_tensor(halves(h[:, m, :]), pv(t0 + m), halves(h[:, m, :]), ALU.add)\
                       .then_inc(h_done, 1)
                    dve.wait_ge(h_done, base + m + 1)
                    dve.nop().then_inc(psum_free, 1)
                    if m:
                        sum_sq(n, m - 1)
                sum_sq(n, 7)

            def ffn(l, n):
                def up_part(q):
                    for j in range(8):
                        t = T_FFN[l] + j
                        dve.wait_ge(psum_full, q * 16 + (t + 1))
                        if j >= 2:
                            dve.wait_ge(hid_ready, q * 8 + (32 * l + j - 1))
                        dve.scalar_tensor_tensor(halves(rbuf[:, j % 2, :]), pv(t), 0.0, halves(rstd[:]),
                                                 ALU.max, ALU.mult).then_inc(psum_free, 1)
                    dve.wait_ge(hid_ready, q * 8 + (32 * l + 8))

                with nc.Fori(0, 3, engines=[dve.engine]) as q:
                    up_part(q)
                    for m in range(8):
                        t = T_FFN[l] + 8 + m
                        dve.wait_ge(psum_full, q * 16 + (t + 1))
                        dve.wait_ge(h_done, q * 8 + (H_FFN[l] + m - 7))
                        dve.tensor_tensor(halves(h[:, m, :]), pv(t), halves(h[:, m, :]), ALU.add)\
                           .then_inc(h_done, 1)
                        dve.wait_ge(h_done, q * 8 + (H_FFN[l] + m + 1))
                        dve.nop().then_inc(psum_free, 1)
                up_part(3)
                add_h(T_FFN[l] + 56, H_FFN[l] + 24, n)

            def ple(l, n_root, n):
                for m in range(8):
                    full(T_PP[l] + m)
                    dve.tensor_copy(halves(pp[:, m, :]), pv(T_PP[l] + m)).then_inc(psum_free, 1)
                norm_root(n_root, T_NP[l], rstd[:], D)
                for m in range(9):
                    if m < 8:
                        t = T_GATE[l] + m
                        full(t)
                        dve.tensor_tensor(halves(rbuf[:, m % 2, :]), pv(t), halves(rstd[:]), ALU.mult)\
                           .then_inc(psum_free, 1)
                    if m:
                        k = m - 1
                        dve.wait_ge(act_x, (5 if l == 0 else 5 + 8 + 24) + k + 1)
                        dve.wait_ge(h_done, H_GATE[l] + k - 7)
                        link(dve.tensor_tensor(pp[:, k, :], pp[:, k, :], rbuf[:, k % 2, :], ALU.mult))
                        dve.tensor_tensor(h[:, k, :], h[:, k, :], pp[:, k, :], ALU.add).then_inc(h_done, 1)
                        if k:
                            sum_sq(n, k - 1)
                sum_sq(n, 7)

            dve.wait_ge(consts, 2)
            for m in range(8):
                sum_sq(0, m)
            norm_root(0, T_N0, rstd[:], D)
            for m in range(18):
                t = T_INAB + m
                full(t)
                dve.tensor_tensor(halves(stage[:, m, :]), pv(t), halves(rstd[:]), ALU.mult).then_inc(psum_free, 1)
            dve.wait_ge(psum_free, T_NQ)
            dve.wait_ge(c_loaded, 128)
            norm_root(1, T_NQ, sq[:, 0, :], QR)
            norm_root(2, T_NKV, sq[:, 1, :], R)
            for i in range(3):
                link(dve.scalar_tensor_tensor(stage[:, 12 + i, :], stage[:, 12 + i, :], qgain(i), sq[:, 0, :],
                                              ALU.mult, ALU.mult))
            for i in range(2):
                link(dve.scalar_tensor_tensor(stage[:, 15 + i, :], stage[:, 15 + i, :], kvgain(i), sq[:, 1, :],
                                              ALU.mult, ALU.mult))
            dve.nop().then_inc(dve_x, 4)
            kx = stage[:, 17, :]
            link(dve.tensor_tensor(rbuf[64:96, 0, :], kx[0:32, :], rope[0:32, 4, :], ALU.mult))
            link(dve.tensor_tensor(rbuf[64:96, 1, :], kx[32:64, :], rope[32:64, 5, :], ALU.mult))
            link(dve.tensor_tensor(ssum[64:96, :], rbuf[64:96, 0, :], rbuf[64:96, 1, :], ALU.add))
            for c in range(4):
                link(dve.tensor_tensor(up[:, c, 2:UPS], stage[:, 4 + c, 0:TP], stage[:, c, 0:TP], ALU.mult))
                link(dve.tensor_tensor(ups(c, 2, 4), tok(stage[:, 4 + c, TP:T]), tok(stage[:, c, TP:T]), ALU.mult))
                link(dve.tensor_scalar(acc[:, 0:TP], up[:, c, 0:TP], tap(0, c), None, ALU.mult))
                link(dve.tensor_scalar(tok(acc[:, TP:T]), ups(c, 0, 4), tap(0, c), None, ALU.mult))
                for i in (1, 2):
                    link(dve.scalar_tensor_tensor(acc[:, 0:TP], up[:, c, i:i + TP], tap(i, c), acc[:, 0:TP],
                                                  ALU.mult, ALU.add))
                    link(dve.scalar_tensor_tensor(tok(acc[:, TP:T]), ups(c, i, 4), tap(i, c), tok(acc[:, TP:T]),
                                                  ALU.mult, ALU.add))
                link(dve.tensor_tensor(B[:, c, :], acc, stage[:, 8 + c, :], ALU.mult))
            dve.wait_ge(psum_full, T_NKV + 1)
            for c in range(4):
                full(T_UQ + c)
                link(dve.tensor_copy(halves(Q[0:64, 2 * c, :]), pv(T_UQ + c)[0:64]))
                link(dve.tensor_copy(halves(Q[0:64, 2 * c + 1, :]), pv(T_UQ + c)[64:128]))
                dve.nop().then_inc(psum_free, 1)
            for c in range(2):
                for s in range(2):
                    t = T_UQ + 4 + 2 * c + s
                    full(t)
                    link(dve.tensor_tensor(halves(rbuf[:, s, :]), pv(t), halves(rope[:, 4 + s, :]), ALU.mult))
                    dve.nop().then_inc(psum_free, 1)
                for j in range(4):
                    link(dve.tensor_tensor(Q[64:96, 4 * c + j, :], rbuf[32 * j:32 * j + 32, 0, :],
                                           rbuf[32 * j:32 * j + 32, 1, :], ALU.add))
            for hd in range(H):
                link(dve.tensor_copy(K[64:96, hd, :], ssum[64:96, 0:TP]))
            for c in range(4):
                full(T_UK + c)
                link(dve.tensor_copy(K[0:64, 2 * c, :], slot(T_UK + c)[0:64, 0, :]))
                link(dve.tensor_copy(K[0:64, 2 * c + 1, :], slot(T_UK + c)[64:128, 0, :]))
                dve.nop().then_inc(psum_free, 1)
            for i in range(4):
                full(T_UV + i)
                dve.tensor_copy(vtok[:, i, :], slot(T_UV + i)[:, 0, :]).then_inc(psum_free, 1)
            dve.wait_ge(psum_free, T_OUTAB)
            dve.nop().then_inc(conv_done, 1)
            for n in range(NPR + 3):
                if n < NPR:
                    i = n % 4
                    sc = psum[:, n % 3, 0:(i + 1) * P]
                    dve.wait_ge(sc_full, n + 1)
                    link(dve.tensor_tensor(sc[:, i * P:], sc[:, i * P:], cmask, ALU.add))
                    if n >= 2:
                        dve.wait_ge(pexp, n - 1)
                    link(dve.tensor_reduce(small[:, n % 2:n % 2 + 1], sc, AX, ALU.max))
                    dve.tensor_scalar(small[:, 8 + n % 2:9 + n % 2], small[:, n % 2:n % 2 + 1], -SCALE, None,
                                      ALU.mult).then_inc(pmax, 1)
                if 1 <= n < NPR + 1:
                    m = n - 1
                    i = m % 4
                    dve.wait_ge(pexp, m + 1)
                    link(dve.reciprocal(small[:, 16 + m % 2:17 + m % 2], small[:, 12 + m % 2:13 + m % 2]))
                    dve.tensor_scalar(Pp[:, m % 2, 0:(i + 1) * P], Pp[:, m % 2, 0:(i + 1) * P],
                                      small[:, 16 + m % 2:17 + m % 2], None, ALU.mult).then_inc(pnorm, 1)
                if n >= 3:
                    m = n - 3
                    hd, i = divmod(m, 4)
                    r = slice(64 * (hd % 2), 64 * (hd % 2) + 64)
                    dve.wait_ge(y_full, m + 1)
                    dve.tensor_copy(B[r, 4 + hd // 2, i * P:(i + 1) * P], psum[r, 5 + m % 2, 0:P]).then_inc(y_free, 1)
            dve.wait_ge(ql_full, 1)
            re = lambda x: x.rearrange("p (b h t) -> p b h t", b=NB, h=H)
            for c in range(2):
                link(dve.tensor_copy(re(qlat[:, c, :]),
                                     psum[:, c, 0:256].rearrange("p (h b t) -> p b h t", h=H, b=NB)))
            dve.tensor_copy(re(qpe), Q[64:96, :, TP:T].rearrange("p h (b t) -> p b h t", b=NB)).then_inc(ql_ready, 1)
            dve.tensor_copy(kpe_new, ssum[64:96, TP:T]).then_inc(ql_ready, 1)
            dve.tensor_copy(ckv_tok, psum[0:32, 7, 0:256]).then_inc(ql_ready, 1)
            for g in range(2):
                dve.wait_ge(s_full, g + 1)
                if g:
                    dve.wait_ge(st_full, 5)
                link(dve.scalar_tensor_tensor(Ps[:, PAST:PW], psum[:, 4, 0:32], SCALE, smask[:, g, :],
                                              ALU.mult, ALU.add))
                link(dve.tensor_reduce(small[:, 24:25], Ps[:, PAST:PW], AX, ALU.max))
                link(dve.tensor_reduce(small[:, 25:26], psum[:, 0:4, :].rearrange("p a n -> p (a n)"), AX, ALU.max))
                link(dve.tensor_scalar(small[:, 26:27], small[:, 25:26], SCALE, small[:, 24:25], ALU.mult, ALU.max))
                dve.tensor_scalar(small[:, 20:21], small[:, 26:27], -1.0, None, ALU.mult).then_inc(s_soft, 2)
                dve.wait_ge(pexp, NPR + 2 * g + 2)
                link(dve.tensor_tensor(small[:, 27:28], small[:, 22:23], small[:, 23:24], ALU.add))
                link(dve.reciprocal(small[:, 28:29], small[:, 27:28]))
                dve.tensor_scalar(Ps[:, :], Ps[:, :], small[:, 28:29], None, ALU.mult).then_inc(s_soft, 2)
                for bb in range(4):
                    b = 4 * g + bb
                    dve.wait_ge(so_full, b + 1)
                    dve.tensor_copy(olat[:, :, 32 * b:32 * b + 32],
                                    psum[:, 7, 0:64].rearrange("p (c r) -> p c r", c=2)).then_inc(so_ready, 1)
            dve.wait_ge(sy_full, 1)
            dve.tensor_copy(B[:, 4:8, TP:T], psum[:, 7, 0:128].rearrange("p (c r) -> p c r", c=4)).then_inc(sy_ready, 1)

            dve.wait_ge(stored, 112)
            add_h(T_OUTAB, H_OUTAB, 1)
            norm_root(3, T_N1, rstd[:], D)
            ffn(0, 2)
            ple(0, 4, 3)
            norm_root(5, T_N3, rstd[:], D)
            for m in range(16):
                t = T_INC + m
                full(t)
                if m >= 2:
                    dve.wait_ge(act_x, 5 + 8 + m - 1)
                dve.tensor_tensor(halves(rbuf[:, m % 2, :]), pv(t), halves(rstd[:]), ALU.mult).then_inc(psum_free, 1)
            dve.wait_ge(spw_loaded, 48)
            for g in range(8):
                link(dve.tensor_tensor(wsM[:, g, :], wsT[:, g, :], tri, ALU.mult))
                link(dve.tensor_tensor(wsSM[:, g, :], wsS[:, g, :], bmask, ALU.mult))
            norm_root(6, T_NV, sq[:, 0, :], D)
            for m in range(8):
                link(dve.scalar_tensor_tensor(v[:, m, :], v[:, m, :], gain(7, m), sq[:, 0, :], ALU.mult, ALU.mult))
            dve.nop().then_inc(dve_x, 1)
            for g in range(8):
                t = T_SP + 2 * g
                full(t)
                link(dve.tensor_copy(vtk[:, :, g * P:(g + 1) * P],
                                     slot(t)[:, 0, :].rearrange("p (i n) -> p i n", i=4)))
                link(dve.tensor_copy(vts[:, g * P:(g + 1) * P], slot(t)[0:32, 1, 0:P]))
                dve.nop().then_inc(psum_free, 1)
                t += 1
                full(t)
                u = stage[:, 8 + g, :]
                b4 = bias[:, g, 0:P]
                for i in range(4):
                    link(dve.tensor_tensor(rbuf[:, 0, i * P:(i + 1) * P], slot(t)[:, 0, i * P:(i + 1) * P], b4,
                                           ALU.add))
                link(dve.tensor_tensor(rbuf[:, 0, TP:T], slot(t)[:, 1, 0:32], bias[:, g, P:P + 32], ALU.add))
                link(dve.tensor_tensor(HID[1][:, g, :], rbuf[:, 0, :], u, ALU.mult))
                dve.nop().then_inc(psum_free, 1)
            add_h(T_OUTC, H_OUTC, 4)
            norm_root(7, T_N4, rstd[:], D)
            ffn(1, 5)
            ple(1, 8, 6)
            norm_root(9, T_NF, rstd[:], D)
            dve.wait_ge(x_ready, 56)
            for m in range(8):
                dve.tensor_tensor(A[:, m, :], A[:, m, :], rstd[:], ALU.mult).then_inc(dve_x, 1)


OUTS = {"yT": (D, T), "ckvT": (R, T), "kpeT": (ROPE, T), "convp": (P, 4, 2), "convs": (P, 4, NB, 2), "vT": (D, TS)}


def lay_out(i):
    n = {k: np.asarray(v) for k, v in i.items()}
    f = np.float32

    def chunks(w, k):
        return w.reshape(k, P, -1).transpose(1, 0, 2).reshape(P, -1)

    def units(w):
        return [chunks(w[:, c:c + 256], KD) for c in range(0, w.shape[1], 256)]

    win = n["w_in_ab"][0]
    swap = lambda w: w.reshape(w.shape[0], -1, 2, ROPE // 2)[:, :, ::-1, :].reshape(w.shape)
    pe = win[:, -ROPE:]
    win = np.concatenate([win, swap(pe), np.zeros((D, N_INAB * 256 - win.shape[1] - ROPE), f)], 1)
    w = units(win) + units(n["w_out_ab"][0])

    def ffn_ple(l):
        out = []
        for q in range(4):
            out += units(n["w_ff1"][l][:, D * q:D * q + D]) + units(n["w_ff2"][l][D * q:D * q + D])
        return out + [chunks(n["w_ple"][l], 2)] + units(n["w_ple_gate"][l])

    w += ffn_ple(0) + units(n["w_in_c"][0]) + units(n["w_out_c"][0]) + ffn_ple(1)
    uq = n["w_uq"][0].reshape(QR, H, NOPE + ROPE)
    uqp = uq[:, :, NOPE:].reshape(QR, H * ROPE)
    sw = swap(uqp)
    uq = np.concatenate([uq[:, :, :NOPE].reshape(QR, -1), uqp[:, :P], sw[:, :P], uqp[:, P:], sw[:, P:]], 1)
    uk = n["w_uk"][0]
    cols = lambda g, k: g.reshape(k, P).T
    gains = np.zeros((P, 84), f)
    for j, g in enumerate([n["norm_mix"][0], n["norm_ffn"][0], n["norm_ple"][0], n["norm_mix"][1],
                           n["norm_ffn"][1], n["norm_ple"][1], n["norm_f"], n["v_norm"][0]]):
        gains[:, 8 * j:8 * j + 8] = cols(g, 8)
    gains[:, 64:67] = cols(n["q_norm"][0], 3)
    gains[:, 67:69] = cols(n["kv_norm"][0], 2)
    for t in range(3):
        gains[:, 69 + 4 * t:73 + 4 * t] = cols(n["conv_w"][0][t], 4)
    masks = np.zeros((P, 2 * P + 96), f)
    r = np.arange(P)
    masks[:, :P] = np.where(r[None, :] <= r[:, None], 0, -3e38)
    tk = np.arange(TS)
    for g in range(2):
        ok = (tk[None, :] // TD == 4 * g + r[:, None] // 32) & (tk[None, :] % TD <= r[:, None] % TD)
        masks[:, P + 32 * g:P + 32 * g + 32] = np.where(ok, 0, -3e38)
    masks[:32, P + 64:P + 96] = (tk[None, :] // TD == tk[:, None] // TD) & (tk[None, :] >= tk[:, None])
    masks[:, P + 96:] = r[None, :] >= r[:, None]
    pos = np.concatenate([np.arange(TP), PAST + np.tile(np.arange(TD), NB)]).astype(f)
    inv = (f(10000.0) ** (-np.arange(0, ROPE, 2, dtype=f) / f(ROPE))).astype(f)
    ang = (pos[None, :] * inv[np.arange(P) % 16][:, None]).astype(f)
    sign = np.where(np.arange(P) % 32 < 16, -1, 1).astype(f)[:, None]
    rope = np.stack([np.cos(ang), sign * np.sin(ang)], 1).astype(f)
    tokens = lambda p, s: np.concatenate([p.reshape(TP, -1), s.reshape(TS, -1)], 0).T
    pool = n["cache_ckv"][0]
    ws = n["w_s"][0]
    out = {
        "xT": tokens(n["x_prompt"], n["x_sample"]),
        "gains": gains, "ident": np.eye(P, dtype=f), "masks": masks, "rope": rope,
        "state": n["state_conv"][0].transpose(2, 0, 1).reshape(4, P, NB, 2).transpose(1, 0, 2, 3),
        "weights": np.stack(w),
        "attw": np.concatenate([chunks(uq, 3), chunks(uk.reshape(R, -1), 2), chunks(n["w_uv"][0].reshape(R, -1), 2)], 1),
        "wukT": uk.transpose(2, 1, 0).reshape(NOPE, -1),
        "page_table": n["page_table"].reshape(1, -1),
        "keysT": pool.transpose(0, 2, 1).reshape(POOL, 2, P, PAGE).transpose(0, 2, 1, 3).reshape(POOL, P, 2 * PAGE),
        "kpesT": n["cache_kpe"][0].transpose(0, 2, 1),
        "rows": pool,
        "pemb": np.stack([chunks(tokens(n["p_prompt"][l], n["p_sample"][l]), 2) for l in range(2)]),
        "wsS": np.tile(ws[:, :TD, :TD].transpose(2, 0, 1), (NB, 1, NB)),
        "wsT": ws.transpose(2, 0, 1),
        "bias": np.concatenate([n["b_s"][0], np.tile(n["b_s"][0][:, :TD], (1, NB))], 1).reshape(1, -1),
    }
    return {k: np.ascontiguousarray(x) for k, x in out.items()}


def kernel(**inputs):
    import concourse.bacc as bacc
    from concourse.bass_utils import run_bass_kernel_spmd

    arrays = lay_out(inputs)
    nc = bacc.Bacc("TRN2", target_bir_lowering=False, num_devices=1)
    aps = {k: nc.dram_tensor(f"in_{k}", x.shape, mybir.dt.from_np(x.dtype), kind="ExternalInput").ap()
           for k, x in arrays.items()}
    for k, shape in OUTS.items():
        aps[k] = nc.dram_tensor(f"out_{k}", shape, mybir.dt.float32, kind="ExternalOutput").ap()
    build(nc, aps)
    r = run_bass_kernel_spmd(nc, [{f"in_{k}": x for k, x in arrays.items()}], core_ids=[0]).results[0]
    got = {k: np.asarray(r[f"out_{k}"]) for k in OUTS}
    y, c, kp, v = got["yT"].T, got["ckvT"].T, got["kpeT"].T, got["vT"].T
    conv = lambda x, b: x.reshape(P, 4, b, 2).transpose(2, 3, 1, 0).reshape(1, b, 2, CW)
    return (y[:TP].reshape(1, TP, D), y[TP:].reshape(NB, TD, D), conv(got["convp"], 1), conv(got["convs"], NB),
            c[:TP].reshape(1, 1, TP, R), kp[:TP].reshape(1, 1, TP, ROPE), c[TP:].reshape(1, NB, TD, R),
            kp[TP:].reshape(1, NB, TD, ROPE), v.reshape(1, NB, TD, D))
```
